# Optimizing a Trainium2 kernel written in Bass

```python
import math
import jax, jax.numpy as jnp
from jax import lax
import numpy as np

D_MODEL = 2048
BATCH = 1
SEQ = 256
DEPTH = 2
DEC_BATCH = 8
DEC_SEQ = 1
PAST_LEN = 2048
PAGE_SIZE = 128

N_GROUPS = 4
W_GROUP = D_MODEL // N_GROUPS
N_PROJ = 11
CONV_A_WIDTH = 31
CONV_B_WIDTH = 3
CONV_C_WIDTH = 4
CONV_FFN_WIDTH = 3
LRU_HEADS = 4
LRU_HEAD_DIM = W_GROUP // LRU_HEADS
LRU_C = 8.0
RET_HEADS = 4
RET_HEAD_DIM = W_GROUP // RET_HEADS
RET_CHUNK = 128
ROPE_BASE = 10000.0
D_FF = 5632
EPS = 1e-6

kernel_name = "hymba_style_conformer_shortconv_rglru_retention_decoder_step"

def rmsnorm(x, g):
    xf = x.astype(jnp.float32)
    y = xf * lax.rsqrt(jnp.mean(xf * xf, axis=-1, keepdims=True) + EPS)
    return (y * g.astype(jnp.float32)).astype(x.dtype)

def layernorm(x, g, b):
    xf = x.astype(jnp.float32)
    mu = jnp.mean(xf, axis=-1, keepdims=True)
    xc = xf - mu
    y = xc * lax.rsqrt(jnp.mean(xc * xc, axis=-1, keepdims=True) + EPS)
    return (y * g.astype(jnp.float32) + b.astype(jnp.float32)).astype(x.dtype)

def causal_dwconv(x, buf, w):
    width, ch = w.shape
    xp = jnp.concatenate([buf.astype(x.dtype), x], axis=1)
    y = lax.conv_general_dilated(xp, w[:, None, :].astype(x.dtype), window_strides=(1,), padding='VALID',
                                 dimension_numbers=('NWC', 'WIO', 'NWC'), feature_group_count=ch)
    new_buf = xp[:, xp.shape[1] - (width - 1):]
    return y, new_buf

def rope(t, pos):
    half = t.shape[-1] // 2
    inv = ROPE_BASE ** (-jnp.arange(half, dtype=jnp.float32) / half)
    ang = pos.astype(jnp.float32)[:, None] * inv[None, :]
    cos = jnp.cos(ang)[None, :, None, :]
    sin = jnp.sin(ang)[None, :, None, :]
    t1, t2 = t[..., :half], t[..., half:]
    return jnp.concatenate([t1 * cos - t2 * sin, t1 * sin + t2 * cos], axis=-1)

def rglru(xr, r, i, lam, h0):
    log_a = -LRU_C * r * jax.nn.softplus(-lam)
    a = jnp.exp(log_a)
    b = jnp.sqrt(jnp.maximum(-jnp.expm1(2.0 * log_a), 0.0)) * (i * xr)

    def combine(c1, c2):
        a1, b1 = c1
        a2, b2 = c2
        return a1 * a2, a2 * b1 + b2

    a_cum, b_cum = lax.associative_scan(combine, (a, b), axis=1)
    h = a_cum * h0[:, None, :] + b_cum
    return h, h[:, -1]

def retention(q, k, v, s0):
    bsz, seqlen, nh, dh = q.shape
    chunk = RET_CHUNK if seqlen % RET_CHUNK == 0 else seqlen
    n = seqlen // chunk
    log_g = jnp.log(1.0 - 2.0 ** (-5.0 - jnp.arange(nh, dtype=jnp.float32)))
    idx = jnp.arange(chunk, dtype=jnp.float32)
    rel = idx[:, None] - idx[None, :]
    decay_mask = jnp.where(rel >= 0, jnp.exp(log_g[:, None, None] * jnp.maximum(rel, 0.0)), 0.0)
    inner_decay = jnp.exp(log_g[:, None] * (idx + 1.0))[None, :, :, None]
    state_decay = jnp.exp(log_g[:, None] * (chunk - 1.0 - idx))[None, :, :, None]
    chunk_decay = jnp.exp(log_g * chunk)[None, :, None, None]

    def to_chunks(t):
        return t.reshape(bsz, n, chunk, nh, dh).transpose(1, 0, 3, 2, 4)

    def step(s, qkv):
        qc, kc, vc = qkv
        scores = jnp.einsum('bhid,bhjd->bhij', qc, kc) * decay_mask
        o = jnp.einsum('bhij,bhjv->bhiv', scores, vc) + jnp.einsum('bhid,bhdv->bhiv', qc, s) * inner_decay
        s = s * chunk_decay + jnp.einsum('bhjd,bhjv->bhdv', kc * state_decay, vc)
        return s, o

    s_fin, o = lax.scan(step, s0, (to_chunks(q), to_chunks(k), to_chunks(v)))
    o = o.transpose(1, 0, 3, 2, 4).reshape(bsz, seqlen, nh, dh)
    return o, s_fin

def hybrid_layer(x, pos, st, wl):
    conv_a, conv_b, conv_c, lru_h, ret_s, conv_ffn = st
    (g_mix, w_in, w_conv_a, ln_a_g, ln_a_b, w_conv_b, w_conv_c, b_conv_c, w_gate_a, b_gate_a,
     w_gate_x, b_gate_x, lru_lambda, w_out, g_ffn, w_ffn_gate, w_ffn_up, w_conv_ffn, w_ffn_down) = wl
    bsz, seqlen, _ = x.shape
    f32 = jnp.float32
    h = rmsnorm(x, g_mix)
    z = h @ w_in
    a_v, a_g, b_b, b_c, b_x, c_g, c_x, d_q, d_k, d_v, d_g = jnp.split(z, N_PROJ, axis=-1)

    y_a, new_conv_a = causal_dwconv(a_v * jax.nn.sigmoid(a_g), conv_a, w_conv_a)
    y_a = jax.nn.silu(layernorm(y_a, ln_a_g, ln_a_b))

    y_b, new_conv_b = causal_dwconv(b_c * b_x, conv_b, w_conv_b)
    y_b = b_b * y_b

    xr, new_conv_c = causal_dwconv(c_x, conv_c, w_conv_c)
    xr = (xr + b_conv_c).astype(f32)
    xh = xr.reshape(bsz, seqlen, LRU_HEADS, LRU_HEAD_DIM)
    r = jax.nn.sigmoid(jnp.einsum('blhi,hij->blhj', xh, w_gate_a.astype(f32)).reshape(bsz, seqlen, W_GROUP) + b_gate_a.astype(f32))
    ig = jax.nn.sigmoid(jnp.einsum('blhi,hij->blhj', xh, w_gate_x.astype(f32)).reshape(bsz, seqlen, W_GROUP) + b_gate_x.astype(f32))
    h_seq, new_h = rglru(xr, r, ig, lru_lambda.astype(f32), lru_h.astype(f32))
    y_c = h_seq.astype(x.dtype) * jax.nn.gelu(c_g)

    q = rope(d_q.astype(f32).reshape(bsz, seqlen, RET_HEADS, RET_HEAD_DIM), pos)
    k = rope(d_k.astype(f32).reshape(bsz, seqlen, RET_HEADS, RET_HEAD_DIM), pos) * (RET_HEAD_DIM ** -0.5)
    v = d_v.astype(f32).reshape(bsz, seqlen, RET_HEADS, RET_HEAD_DIM)
    o, new_s = retention(q, k, v, ret_s.astype(f32))
    o = o * lax.rsqrt(jnp.mean(o * o, axis=-1, keepdims=True) + EPS)
    y_d = jax.nn.silu(d_g) * o.reshape(bsz, seqlen, W_GROUP).astype(x.dtype)

    mix = jnp.concatenate([y_a, y_b, y_c, y_d], axis=-1)
    x = x + mix @ w_out

    h2 = rmsnorm(x, g_ffn)
    gpre, new_conv_ffn = causal_dwconv(h2 @ w_ffn_gate, conv_ffn, w_conv_ffn)
    x = x + (jax.nn.silu(gpre) * (h2 @ w_ffn_up)) @ w_ffn_down
    dt = x.dtype
    return x, (new_conv_a.astype(dt), new_conv_b.astype(dt), new_conv_c.astype(dt), new_h.astype(dt),
               new_s.astype(dt), new_conv_ffn.astype(dt))

def run_trunk(x, pos, states, weights, g_final):
    new = [[] for _ in states]
    for l in range(DEPTH):
        x, ns = hybrid_layer(x, pos, tuple(s[l] for s in states), tuple(w[l] for w in weights))
        for lst, s in zip(new, ns):
            lst.append(s)
    return rmsnorm(x, g_final), tuple(jnp.stack(lst) for lst in new)

def setup_inputs(seed: int = 0) -> dict:
    key = jax.random.key(seed)
    ks = jax.random.split(key, 32)
    f32 = jnp.float32
    nrm = lambda k, shape, s: jax.random.normal(k, shape, f32) * s
    u = jax.random.uniform(ks[20], (DEPTH, W_GROUP), f32, 0.9, 0.999) ** (1.0 / LRU_C)
    return {
        'x_prompt': nrm(ks[0], (BATCH, SEQ, D_MODEL), 1.0),
        'x_sample': nrm(ks[1], (DEC_BATCH, DEC_SEQ, D_MODEL), 1.0),
        'state_conv_a': nrm(ks[2], (DEPTH, DEC_BATCH, CONV_A_WIDTH - 1, W_GROUP), 0.5),
        'state_conv_b': nrm(ks[3], (DEPTH, DEC_BATCH, CONV_B_WIDTH - 1, W_GROUP), 0.5),
        'state_conv_c': nrm(ks[4], (DEPTH, DEC_BATCH, CONV_C_WIDTH - 1, W_GROUP), 0.5),
        'state_lru_c': nrm(ks[5], (DEPTH, DEC_BATCH, W_GROUP), 0.5),
        'state_ret_d': nrm(ks[6], (DEPTH, DEC_BATCH, RET_HEADS, RET_HEAD_DIM, RET_HEAD_DIM), 0.5),
        'state_conv_ffn': nrm(ks[7], (DEPTH, DEC_BATCH, CONV_FFN_WIDTH - 1, D_FF), 0.5),
        'g_mix': 1.0 + nrm(ks[8], (DEPTH, D_MODEL), 0.02),
        'w_in': nrm(ks[9], (DEPTH, D_MODEL, N_PROJ * W_GROUP), D_MODEL ** -0.5),
        'w_conv_a': nrm(ks[10], (DEPTH, CONV_A_WIDTH, W_GROUP), CONV_A_WIDTH ** -0.5),
        'ln_a_g': 1.0 + nrm(ks[11], (DEPTH, W_GROUP), 0.02),
        'ln_a_b': nrm(ks[12], (DEPTH, W_GROUP), 0.02),
        'w_conv_b': nrm(ks[13], (DEPTH, CONV_B_WIDTH, W_GROUP), CONV_B_WIDTH ** -0.5),
        'w_conv_c': nrm(ks[14], (DEPTH, CONV_C_WIDTH, W_GROUP), CONV_C_WIDTH ** -0.5),
        'b_conv_c': nrm(ks[15], (DEPTH, W_GROUP), 0.02),
        'w_gate_a': nrm(ks[16], (DEPTH, LRU_HEADS, LRU_HEAD_DIM, LRU_HEAD_DIM), LRU_HEAD_DIM ** -0.5),
        'b_gate_a': nrm(ks[17], (DEPTH, W_GROUP), 0.1),
        'w_gate_x': nrm(ks[18], (DEPTH, LRU_HEADS, LRU_HEAD_DIM, LRU_HEAD_DIM), LRU_HEAD_DIM ** -0.5),
        'b_gate_x': nrm(ks[19], (DEPTH, W_GROUP), 0.1),
        'lru_lambda': jnp.log(u / (1.0 - u)),
        'w_out': nrm(ks[21], (DEPTH, D_MODEL, D_MODEL), D_MODEL ** -0.5),
        'g_ffn': 1.0 + nrm(ks[22], (DEPTH, D_MODEL), 0.02),
        'w_ffn_gate': nrm(ks[23], (DEPTH, D_MODEL, D_FF), D_MODEL ** -0.5),
        'w_ffn_up': nrm(ks[24], (DEPTH, D_MODEL, D_FF), D_MODEL ** -0.5),
        'w_conv_ffn': nrm(ks[25], (DEPTH, CONV_FFN_WIDTH, D_FF), CONV_FFN_WIDTH ** -0.5),
        'w_ffn_down': nrm(ks[26], (DEPTH, D_FF, D_MODEL), D_FF ** -0.5),
        'g_final': 1.0 + nrm(ks[27], (D_MODEL,), 0.02),
    }

def reference(x_prompt, x_sample, state_conv_a, state_conv_b, state_conv_c, state_lru_c, state_ret_d, state_conv_ffn,
              g_mix, w_in, w_conv_a, ln_a_g, ln_a_b, w_conv_b, w_conv_c, b_conv_c, w_gate_a, b_gate_a, w_gate_x, b_gate_x,
              lru_lambda, w_out, g_ffn, w_ffn_gate, w_ffn_up, w_conv_ffn, w_ffn_down, g_final):
    weights = (g_mix, w_in, w_conv_a, ln_a_g, ln_a_b, w_conv_b, w_conv_c, b_conv_c, w_gate_a, b_gate_a,
               w_gate_x, b_gate_x, lru_lambda, w_out, g_ffn, w_ffn_gate, w_ffn_up, w_conv_ffn, w_ffn_down)
    bp = x_prompt.shape[0]
    dt = x_prompt.dtype
    zero_states = (
        jnp.zeros((DEPTH, bp, CONV_A_WIDTH - 1, W_GROUP), dt),
        jnp.zeros((DEPTH, bp, CONV_B_WIDTH - 1, W_GROUP), dt),
        jnp.zeros((DEPTH, bp, CONV_C_WIDTH - 1, W_GROUP), dt),
        jnp.zeros((DEPTH, bp, W_GROUP), dt),
        jnp.zeros((DEPTH, bp, RET_HEADS, RET_HEAD_DIM, RET_HEAD_DIM), dt),
        jnp.zeros((DEPTH, bp, CONV_FFN_WIDTH - 1, D_FF), dt),
    )
    pos_p = jnp.arange(x_prompt.shape[1], dtype=jnp.int32)
    pos_s = PAST_LEN + jnp.arange(x_sample.shape[1], dtype=jnp.int32)
    y_prompt, (p_conv_a, p_conv_b, p_conv_c, p_lru_c, p_ret_d, p_conv_ffn) = run_trunk(
        x_prompt, pos_p, zero_states, weights, g_final)
    y_sample, (s_conv_a, s_conv_b, s_conv_c, s_lru_c, s_ret_d, s_conv_ffn) = run_trunk(
        x_sample, pos_s, (state_conv_a, state_conv_b, state_conv_c, state_lru_c, state_ret_d, state_conv_ffn),
        weights, g_final)
    return (y_prompt, y_sample, p_conv_a, p_conv_b, p_conv_c, p_lru_c, p_ret_d, p_conv_ffn,
            s_conv_a, s_conv_b, s_conv_c, s_lru_c, s_ret_d, s_conv_ffn)


_drawn_inputs = setup_inputs


def setup_inputs(seed=0):
    import zlib

    import numpy as np

    out = dict(_drawn_inputs(seed))
    spreads = {}
    factors = {'ln_a_g': 3.715, 'ln_a_b': 2.862, 'g_final': 8.006, 'b_gate_a': 3.026}
    for name, (base, spread) in spreads.items():
        noise = np.random.default_rng([zlib.crc32(name.encode()), seed]).standard_normal(out[name].shape)
        drawn = base * np.exp(spread * noise) if base else spread * noise
        out[name] = __import__('jax').numpy.asarray(drawn.astype(out[name].dtype))
    for name, factor in factors.items():
        out[name] = (out[name] * factor).astype(out[name].dtype)
    return out
```

```python
from contextlib import ExitStack

import concourse.bass as bass
from concourse import mybir

F32 = mybir.dt.float32
F32R = mybir.dt.float32r
ALU = mybir.AluOpType
ACT = mybir.ActivationFunctionType
AX = mybir.AxisListType.X

DEPTH, D_MODEL, SEQ, B = 2, 2048, 256, 8
P = 128
T = SEQ + B
KT = D_MODEL // P
W_GROUP = D_MODEL // 4
HEADS = W_GROUP // P
D_FF = 5632
FT = D_FF // P
NBLK = FT // 4
WA, WB, WC, WF = 31, 3, 4, 3
CH = 128
EPS = 1e-6

CHUNK = 8 * P
RING = 4
G_IN, G_OUT = 11, 4
G_GATE0 = G_IN + G_OUT
G_UP0 = G_GATE0 + 1
G_LOOP = G_UP0 + 1
G_LAST = G_LOOP + 3 * (NBLK - 1)
GROUPS = G_LAST + 1
CHUNKS = 8 * GROUPS
TILES = 4 * (G_IN + G_OUT) + 8 * NBLK
PAIRS = 8 * NBLK

A_V, A_G, B_B, B_C, B_X, C_G, C_X, D_Q, D_K, D_V, D_G = range(11)
IN_ORDER = [A_V, A_G, D_Q, D_K, D_V, C_X, C_G, D_G, B_C, B_X, B_B]
OUT_ROWS = [0, 1, 2, 3, 12, 13, 14, 15, 8, 9, 10, 11, 4, 5, 6, 7]

PAR = {}
_at = 0
for _name, _n in (("wa", WA), ("wb", WB), ("wc", WC), ("bc", 1), ("lng", 1), ("lnb", 1), ("ba", 1), ("bx", 1),
                  ("lam", 1), ("sb", B * WB), ("sc", B * WC), ("lru", B), ("pa", WA - 1), ("pb", WB - 1),
                  ("pc", WC - 1), ("pl", 1)):
    PAR[_name] = (_at, _at + _n)
    _at += _n
N_PAR = _at
N_PAR_IN = PAR["pa"][0]
STATE0 = PAR["sb"][0]

SIGNALS = dict(
    exp_in=1, lam_exp=1, sum_sq=2, conv_a=1, state_read=3, std=2, ag_sig=4, u_ready=1, q_swap=1, q_rope=1, k_swap=1, k_rope=1,
    kv_turned=1, kt_ready=1, vt_ready=1, scored=1, probs=1, kv8_ready=1, s_summed=1, s1_ready=1,
    o_summed=1, o_ready=1, v_diag=4, outer=4, s_new=4, o8_summed=1, o8_ready=1, o_sq=1, o_sums=1, o_std=1,
    dg_silu=1, yd=1, ln_mean=1, centered=1, ln_sq=1, ln_var=1, ln_std=1, ln_scaled=1, ya=1,
    xr=1, ga=1, gx=1, r_sig=1, i_sig=1, ixr=1, a_exp=1, t_tanh=1, b_sq=1, b_sqrt=1, cg_gelu=1, yc=1, yb=4,
    mix_hi=7, mix_lo=7, x_hi=32, x_lo=32, x_added=8, x_sq=4,
    gate_conv=NBLK, gate_silu=NBLK, h_new=4 * NBLK, h_hi=4 * NBLK, h_lo=4 * NBLK,
)
AHEAD = dict(x_hi=KT, x_lo=KT, x_added=4)


class Signal:

    def __init__(self, sem, per_layer, start=0):
        self.sem, self.per_layer, self.start = sem, per_layer, start

    def at(self, layer, k):
        return layer * self.per_layer + (self.start + k)


def hybrid_step(nc, x_in, w_in_all, par_in, sa_in, wg_in, sr_in, wf_in, fs_in, gains_in, tab_in,
                y_out, par_out, sa_out, rp_out, rs_out, fs_out, fp_out):
    ctx = ExitStack()
    with ctx:
        def sb(name, shape, dt=F32):
            return ctx.enter_context(nc.sbuf_tensor(name, shape, dt))

        def sem(name):
            return ctx.enter_context(nc.semaphore(name))

        x = sb("x", [P, KT, T])
        xh, xl = sb("xh", [P, KT, T], F32R), sb("xl", [P, KT, T], F32R)
        mh, ml = sb("mh", [P, KT, T], F32R), sb("ml", [P, KT, T], F32R)
        hh, hl = sb("hh", [P, 4, T], F32R), sb("hl", [P, 4, T], F32R)
        raw = sb("raw", [P, RING, CHUNK])
        wh, wl = sb("wh", [P, RING, CHUNK], F32R), sb("wl", [P, RING, CHUNK], F32R)
        av, ag, u, q, k = (sb(n, [P, 4, T]) for n in ("av", "ag", "u", "q", "k"))
        v, dg, cg, cx, e = (sb(n, [P, 4, T]) for n in ("v", "dg", "cg", "cx", "e"))
        sa = sb("sa", [P, 1024])
        s_own = sb("s_own", [P, B, CH])
        kv8 = sb("kv8", [B, 2, HEADS, P])
        N_TAB = 2 * T + 2 * HEADS * CH + HEADS + B + 2 * P + 1
        tab = sb("tab", [P, N_TAB])
        gains = sb("gains", [P, 2 * DEPTH + 1, KT])
        par = sb("par", [P, HEADS, N_PAR])
        wf = sb("wf", [P, FT, WF])
        fp = sb("fp", [P, FT, 2])
        rs, ssq, std, tmp = (sb(n, [P, T]) for n in ("rs", "ssq", "std", "tmp"))
        sp = sb("sp", [P, 8, HEADS])

        o = 0
        cos_t = tab[:, o:o + T]; o += T
        sin_t = tab[:, o:o + T]; o += T
        mask_t = tab[:, o:o + HEADS * CH].rearrange("p (h i) -> p h i", h=HEADS); o += HEADS * CH
        inner_t = tab[:, o:o + HEADS * CH].rearrange("p (h i) -> p h i", h=HEADS); o += HEADS * CH
        decay_t = tab[:, o:o + HEADS]; o += HEADS
        batch_t = tab[0:B, o:o + B]; o += B
        ident = tab[:, o:o + P]; o += P
        ones = tab[:, o:o + P]; o += P
        eps_t = tab[:, o:o + 1]

        n_kv = 2 * HEADS * CH
        def flat(t):
            return t[:, :, :].rearrange("p a b -> p (a b)")
        sa_v = sa[:, 0:HEADS * B * WA].rearrange("p (m b j) -> p m b j", m=HEADS, b=B)
        wg = sa[:, 0:1024].rearrange("p (g h j) -> p g h j", g=2, h=HEADS)
        kt_v = flat(ag)[:, 0:n_kv].rearrange("p (c h d) -> p c h d", c=2, h=HEADS)
        rp_v = flat(ag)[:, 0:HEADS * CH].rearrange("p (h d) -> p h d", h=HEADS)
        vt_v = flat(e)[:, 0:n_kv].rearrange("p (c h d) -> p c h d", c=2, h=HEADS)
        pt_v = flat(k)[:, 0:n_kv].rearrange("p (c h i) -> p c h i", c=2, h=HEADS)
        s1_v = flat(dg)[:, 0:HEADS * CH].rearrange("p (h d) -> p h d", h=HEADS)
        vd_v = flat(u)[0:B, 0:B * CH].rearrange("p (b v) -> p b v", b=B)
        s_alt = flat(k)[:, 0:B * CH].rearrange("p (b v) -> p b v", b=B)
        fs_v = flat(dg)[:, 0:FT * B * WF].rearrange("p (f b j) -> p f b j", f=FT, b=B)
        prod_a = flat(e)[:, 0:HEADS * B * WA].rearrange("p (m b j) -> p m b j", m=HEADS, b=B)

        bank = ctx.enter_context(nc.psum_tensor("bank", [P, 8, 512], F32))

        one_tile = [tmp[:, :], std[:, :]]

        def states(h):
            return s_own[:, :, :] if h % 2 == 0 else s_alt

        S = {n: Signal(sem(n), c, AHEAD.get(n, 0)) for n, c in SIGNALS.items()}
        raw_loaded = [sem(f"raw_loaded{i}") for i in range(RING)]
        hi_made, lo_made = sem("hi_made"), sem("lo_made")
        chunk_used = Signal(sem("chunk_used"), CHUNKS, RING)
        bank_empty = Signal(sem("bank_empty"), TILES, 4)
        pair_empty = Signal(sem("pair_empty"), PAIRS, 2)
        gains_loaded, tab_loaded = sem("gains_loaded"), sem("tab_loaded")
        x_loaded = [sem(f"x_loaded{i}") for i in range(4)]
        par_loaded, sa_loaded, wg_loaded, wf_loaded, fs_loaded = (
            sem(n) for n in ("par_loaded", "sa_loaded", "wg_loaded", "wf_loaded", "fs_loaded"))
        s_loaded = [sem("s_loaded0"), sem("s_loaded1")]
        s_stored = [sem("s_stored0"), sem("s_stored1")]
        sa_stored, rp_stored, par_stored, fs_stored, y_stored = (
            sem(n) for n in ("sa_stored", "rp_stored", "par_stored", "fs_stored", "y_stored"))
        final_sum, final_std, y_ready = sem("final_sum"), sem("final_std"), sem("y_ready")

        block = ctx.enter_context(nc.Block())
        ALL = DEPTH * CHUNKS

        def pw(name, m, j=0):
            a = PAR[name][0] + j
            return par[:, m, a:a + 1]

        @block.sync
        def _(sync):
            for i in range(RING):
                sync.dma_start(x[:, 4 * i:4 * i + 4, :], x_in[:, 4 * i:4 * i + 4, :]).then_inc(x_loaded[i], 16)
                sync.dma_start(raw[:, i, :], w_in_all[i, :, :]).then_inc(raw_loaded[i], 16)
            sync.dma_start(tab[:, :], tab_in).then_inc(tab_loaded, 16)
            with sync.Fori(1, ALL // RING) as turn:
                for i in range(RING):
                    sync.wait_ge(lo_made, turn * RING + (i + 1 - RING))
                    sync.dma_start(raw[:, i, :], w_in_all[bass.ds(turn * RING + i, 1), :, :].rearrange("a p n -> p (a n)"))\
                        .then_inc(raw_loaded[i], 16)

        @block.gpsimd
        def _(pool):
            with pool.Fori(0, ALL, RING) as c:
                for i in range(RING):
                    pool.wait_ge(hi_made, c + (i + 1))
                    pool.tensor_tensor(wl[:, i, :], raw[:, i, :], wh[:, i, :].bitcast(F32), ALU.subtract)\
                        .then_inc(lo_made, 1)

        @block.scalar
        def _(act):
            def hi(l, group, j):
                i = j % RING
                act.wait_ge(raw_loaded[i], l * (CHUNKS * 4) + (group * 32 + (j // RING) * 16 + 16))
                act.wait_ge(chunk_used.sem, l * CHUNKS + (group * 8 + (j + 1)))
                act.activation(wh[:, i, :], raw[:, i, :], ACT.Copy).then_inc(hi_made, 1)

            def split_x(kk, gain):
                act.activation(xh[:, kk, :], x[:, kk, :], ACT.Copy, scale=gain(kk)).then_inc(S["x_hi"].sem, 1)

            def std_of(l, n):
                act.wait_ge(S["sum_sq"].sem, S["sum_sq"].at(l, n + 1))
                act.activation(std[:, :], bank[:, 4, 0:T], ACT.Sqrt, scale=1.0 / D_MODEL, bias=eps_t)\
                    .then_inc(S["std"].sem, 1)

            def mix_hi(l, n, t0, nt, src, ready, kr):
                act.wait_ge(ready.sem, ready.at(l, kr))
                act.activation(mh[:, t0:t0 + nt, :], src, ACT.Copy).then_inc(S["mix_hi"].sem, 1)

            def on(name, l, kk=1):
                act.wait_ge(S[name].sem, S[name].at(l, kk))

            def tile_in(l, p):
                act.wait_ge(bank_empty.sem, bank_empty.at(l, p + 1))

            def hh_of(l, blk, m):
                act.wait_ge(S["h_new"].sem, S["h_new"].at(l, blk * 4 + (m + 1)))
                act.activation(hh[:, m, :], v[:, m, :], ACT.Copy).then_inc(S["h_hi"].sem, 1)

            def silu_gate(l, blk):
                act.wait_ge(S["gate_conv"].sem, S["gate_conv"].at(l, blk + 1))
                act.activation(k[:, :, :], k[:, :, :], ACT.Silu).then_inc(S["gate_silu"].sem, 1)

            act.dma_start(gains[:, :, :], gains_in).then_inc(gains_loaded, 16)
            act.wait_ge(gains_loaded, 16)
            for kk in range(KT):
                act.wait_ge(x_loaded[kk // 4], 16)
                split_x(kk, lambda t: gains[:, 0, t:t + 1])

            with act.Fori(0, DEPTH) as l:
                act.dma_start(par[:, :, 0:N_PAR_IN], par_in[bass.ds(l, 1), :, :, :].rearrange("a p m n -> p (a m) n"))\
                    .then_inc(par_loaded, 16)
                act.dma_start(wf[:, :, :], wf_in[bass.ds(l, 1), :, :, :].rearrange("a p m n -> p (a m) n"))\
                    .then_inc(wf_loaded, 16)
                act.dma_start(sa[:, 0:HEADS * B * WA], sa_in[bass.ds(l, 1), :, :].rearrange("a p n -> p (a n)"))\
                    .then_inc(sa_loaded, 16)

                def load_s(h):
                    act.dma_start(states(h), sr_in[bass.ds(l * HEADS + h, 1), :, :, :].rearrange("a p b v -> p (a b) v"))\
                        .then_inc(s_loaded[h % 2], 16)

                def store_s(h):
                    on("s_new", l, h + 1)
                    act.dma_start(rs_out[bass.ds(l * HEADS + h, 1), :, :, :].rearrange("a p b v -> p (a b) v"), states(h))\
                        .then_inc(s_stored[h % 2], 16)

                load_s(0)

                def h_lam():
                    on("exp_in", l)
                    act.activation(sp[:, 1, :], sp[:, 0, :], ACT.Exp).then_inc(S["lam_exp"].sem, 1)

                def h_ag(m):
                    def f():
                        tile_in(l, 4 + m)
                        act.activation(ag[:, m, :], ag[:, m, :], ACT.Sigmoid).then_inc(S["ag_sig"].sem, 1)
                    return f

                def h_store_a():
                    on("u_ready", l)
                    act.dma_start(sa_out[bass.ds(l, 1), :, :].rearrange("a p n -> p (a n)"), sa[:, 0:HEADS * B * WA])\
                        .then_inc(sa_stored, 16)

                def h_load_wg():
                    act.wait_ge(sa_stored, l * 16 + 16)
                    act.dma_start(sa[:, :], wg_in[bass.ds(l, 1), :, :].rearrange("a p n -> p (a n)")).then_inc(wg_loaded, 16)

                def swap(src, p, done, free):
                    def f():
                        tile_in(l, p)
                        on(free, l)
                        act.activation(ag[0:64, :, :], src[64:128, :, :], ACT.Copy)
                        act.activation(ag[64:128, :, :], src[0:64, :, :], ACT.Copy).then_inc(S[done].sem, 1)
                    return f

                def h_vt():
                    on("kv_turned", l)
                    act.activation(vt_v, bank[:, 6:8, :].rearrange("p c (h d) -> p c h d", h=HEADS), ACT.Copy)\
                        .then_inc(S["vt_ready"].sem, 1)

                def h_kv8():
                    on("scored", l)
                    act.activation(kv8[:, :, :, :], bank[0:B, 6:8, :].rearrange("p c (h d) -> p c h d", h=HEADS), ACT.Copy)\
                        .then_inc(S["kv8_ready"].sem, 1)

                def h_rp():
                    on("s1_ready", l)
                    act.dma_start(rp_out[bass.ds(l, 1), :, :, :].rearrange("a p h d -> p (a h) d"), rp_v).then_inc(rp_stored, 16)

                def h_o():
                    on("o_summed", l)
                    for c in range(2):
                        i = act.activation(v[:, :, c * CH:(c + 1) * CH],
                                           bank[:, 4 + c, :].rearrange("p (h i) -> p h i", h=HEADS), ACT.Copy)
                    i.then_inc(S["o_ready"].sem, 1)
                    load_s(1)

                def h_ln_sq():
                    on("centered", l)
                    act.activation(e[:, :, :], av[:, :, :], ACT.Square).then_inc(S["ln_sq"].sem, 1)

                def h_ln_std():
                    on("ln_var", l)
                    act.activation(std[:, :], bank[:, 7, 0:T], ACT.Sqrt, scale=1.0 / W_GROUP, bias=eps_t)\
                        .then_inc(S["ln_std"].sem, 1)

                def h_ya():
                    on("ln_scaled", l)
                    for m in range(4):
                        i = act.activation(av[:, m, :], av[:, m, :], ACT.Silu, bias=pw("lnb", m), scale=pw("lng", m))
                    i.then_inc(S["ya"].sem, 1)
                    mix_hi(l, 0, 0, 4, av[:, :, :], S["ya"], 1)

                def h_dg():
                    tile_in(l, 31)
                    act.activation(dg[:, :, :], dg[:, :, :], ACT.Silu).then_inc(S["dg_silu"].sem, 1)

                def h_o8():
                    on("o8_summed", l)
                    act.activation(v[:, :, SEQ:T], bank[:, 6, 0:HEADS * B].rearrange("p (h b) -> p h b", h=HEADS), ACT.Copy)\
                        .then_inc(S["o8_ready"].sem, 1)
                    on("o8_ready", l)
                    act.activation(q[:, :, :], v[:, :, :], ACT.Square).then_inc(S["o_sq"].sem, 1)

                def h_ostd():
                    on("o_sums", l)
                    i = act.activation(e[:, :, :], bank[:, 4:8, 0:T], ACT.Sqrt, scale=1.0 / CH, bias=eps_t)
                    i.then_inc(S["o_std"].sem, 1)

                def h_gelu():
                    tile_in(l, 27)
                    act.activation(cg[:, :, :], cg[:, :, :], ACT.Gelu_apprx_tanh).then_inc(S["cg_gelu"].sem, 1)

                def gate(dst, got, bias, done):
                    def f():
                        on(got, l)
                        for m in range(4):
                            i = act.activation(dst[:, m, :], bank[:, 4 + m, 0:T], ACT.Sigmoid, bias=pw(bias, m))
                        i.then_inc(S[done].sem, 1)
                    return f

                def h_decay():
                    on("ixr", l)
                    for m in range(4):
                        i = act.activation(ag[:, m, :], q[:, m, :], ACT.Exp, scale=sp[:, 7, m:m + 1])
                    i.then_inc(S["a_exp"].sem, 1)
                    for m in range(4):
                        i = act.activation(e[:, m, :], q[:, m, :], ACT.Tanh, scale=sp[:, 6, m:m + 1])
                    i.then_inc(S["t_tanh"].sem, 1)

                def h_bsqrt():
                    on("b_sq", l)
                    act.activation(q[:, :, :], q[:, :, :], ACT.Sqrt).then_inc(S["b_sqrt"].sem, 1)

                def h_mix(n, t0, nt, src, name, kr):
                    return lambda: mix_hi(l, n, t0, nt, src, S[name], kr)

                def h_s_out():
                    act.wait_ge(s_stored[1], l * 32 + 32)

                def h_store_par():
                    on("yb", l, 4)
                    act.dma_start(par_out[bass.ds(l, 1), :, :, :].rearrange("a p m n -> p (a m) n"),
                                  par[:, :, STATE0:N_PAR]).then_inc(par_stored, 16)

                def h_load_fs():
                    on("yd", l)
                    act.dma_start(flat(dg), fs_in[bass.ds(l, 1), :, :].rearrange("a p n -> p (a n)")).then_inc(fs_loaded, 16)

                def reload_s(h):
                    def f():
                        on("state_read", l, h - 1)
                        act.wait_ge(s_stored[h % 2], l * 32 + (h // 2) * 16)
                        load_s(h)
                    return f

                def gain(n):
                    return lambda t: gains[:, bass.ds(l * 2 + n, 1), t:t + 1].rearrange("p a b -> p (a b)")

                def h_x(kk):
                    tile_in(l, 44 + kk)
                    split_x(kk, gain(1))

                plan = [(0, h_lam), (1, lambda: std_of(l, 0))]
                plan += [(4 + m, h_ag(m)) for m in range(4)]
                plan += [(9, h_store_a), (11, swap(q, 11, "q_swap", "u_ready")), (12, h_load_wg),
                         (15, swap(k, 15, "k_swap", "q_rope")), (20, h_vt), (21, h_kv8), (23, h_rp), (24, h_o),
                         (26, lambda: store_s(0)), (26, h_ln_sq), (27, lambda: store_s(1)), (27, reload_s(2)),
                         (28, h_gelu), (28, reload_s(3)), (29, h_ln_std), (29, lambda: store_s(2)), (30, h_ya),
                         (31, lambda: store_s(3)), (31, h_o8), (32, h_dg), (32.5, h_ostd),
                         (34, gate(q, "ga", "ba", "r_sig")), (35, h_s_out), (35, gate(k, "gx", "bx", "i_sig")),
                         (36, h_decay), (37, h_mix(1, 4, 4, v[:, :, :], "yd", 1)), (38, h_load_fs), (39, h_bsqrt),
                         (40, h_mix(2, 8, 4, e[:, :, :], "yc", 1)), (44, h_store_par)]
                plan += [(40 + m, h_mix(3 + m, 12 + m, 1, u[:, m, :], "yb", m + 1)) for m in range(4)]
                plan += [(44 + kk, lambda kk=kk: h_x(kk)) for kk in range(KT)]
                plan += [(61, lambda: std_of(l, 1)), (63, lambda: silu_gate(l, 0)),
                         (64, lambda: hh_of(l, 0, 0)), (65, lambda: hh_of(l, 0, 1))]
                plan.sort(key=lambda item: item[0])
                for n in range(8 * G_LOOP):
                    hi(l, n // 8, n % 8)
                    while plan and 2 * plan[0][0] + 5 <= n:
                        plan.pop(0)[1]()
                assert not plan

                with act.Fori(1, NBLK) as blk:
                    for n in range(24):
                        i = n % RING
                        act.wait_ge(raw_loaded[i], l * (CHUNKS * 4) + blk * 96 + ((G_LOOP - 3) * 32 + (n // RING) * 16 + 16))
                        act.wait_ge(chunk_used.sem, l * CHUNKS + blk * 24 + ((G_LOOP - 3) * 8 + n + 1))
                        act.activation(wh[:, i, :], raw[:, i, :], ACT.Copy).then_inc(hi_made, 1)
                        if n in (0, 2):
                            hh_of(l, blk - 1, 2 + n // 2)
                        if n == 13:
                            silu_gate(l, blk)
                        if n in (21, 23):
                            hh_of(l, blk, (n - 21) // 2)
                def split_next(kk):
                    act.wait_ge(pair_empty.sem, pair_empty.at(l, (NBLK - 1) * 8 + kk // 2 + 1))
                    split_x(kk, gain(2))
                    if kk % 4 == 3:
                        on("x_added", l, 4 + kk // 4)
                        act.activation(e[:, :, :], x[:, kk - 3:kk + 1, :], ACT.Square).then_inc(S["x_sq"].sem, 1)

                for n in range(8):
                    hi(l, G_LAST, n)
                    if n in (0, 1):
                        hh_of(l, NBLK - 1, 2 + n)
                    if n == 2:
                        act.dma_start(fs_out[bass.ds(l, 1), :, :].rearrange("a p n -> p (a n)"), flat(dg)).then_inc(fs_stored, 16)
                        act.dma_start(fp_out[bass.ds(l, 1), :, :, :].rearrange("a p m n -> p (a m) n"), fp[:, :, :])\
                            .then_inc(fs_stored, 16)
                    if n >= 4:
                        for kk in (2 * (n - 4), 2 * (n - 4) + 1):
                            split_next(kk)
                for kk in range(8, KT):
                    split_next(kk)
                act.wait_ge(fs_stored, l * 32 + 32)
                act.wait_ge(par_stored, l * 16 + 16)
                act.wait_ge(s_stored[0], l * 32 + 32)
                act.wait_ge(s_stored[1], l * 32 + 32)
            act.wait_ge(final_sum, 1)
            act.activation(std[:, :], bank[:, 4, 0:T], ACT.Sqrt, scale=1.0 / D_MODEL, bias=eps_t).then_inc(final_std, 1)
            for n in range(4):
                act.wait_ge(y_ready, n + 1)
                act.dma_start(y_out[:, 4 * n:4 * n + 4, :], x[:, 4 * n:4 * n + 4, :]).then_inc(y_stored, 16)
            act.wait_ge(y_stored, 64)
            act.wait_ge(sa_stored, 16 * DEPTH)
            act.wait_ge(rp_stored, 16 * DEPTH)

        @block.tensor
        def _(pe):
            def on(name, l, kk=1):
                pe.wait_ge(S[name].sem, S[name].at(l, kk))

            def three(out, i, b, rh, rl, first, last):
                w_hi, w_lo = wh[:, i, b * P:(b + 1) * P], wl[:, i, b * P:(b + 1) * P]
                pe.matmul(out, w_hi, rh, start=first, stop=False)
                pe.matmul(out, w_hi, rl, start=False, stop=False)
                return pe.matmul(out, w_lo, rh, start=False, stop=last)

            def stream_tile(chunk, tile, m, rh, rl, before=None):
                pe.wait_ge(bank_empty.sem, tile + (m + 1))
                for j in range(2):
                    pe.wait_ge(lo_made, chunk + (2 * m + j + 1))
                    for b in range(8):
                        kk = 8 * j + b
                        if before is not None:
                            before(kk)
                        i = three(bank[:, m, 0:T], (2 * m + j) % RING, b, rh[:, kk, :], rl[:, kk, :],
                                  kk == 0, kk == 15)
                    i.then_inc(chunk_used.sem, 1)

            def group(chunk, tile, rh, rl, hooks=None, before=None):
                for m in range(4):
                    stream_tile(chunk, tile, m, rh, rl, before if m == 0 else None)
                    for f in (hooks or {}).get(m, ()):
                        f()

            def down(chunk, pair, before=None):
                for j in range(8):
                    pe.wait_ge(pair_empty.sem, pair + (j + 1))
                    pe.wait_ge(lo_made, chunk + (j + 1))
                    for b in range(8):
                        kk = b % 4
                        if j == 0 and b < 4 and before is not None:
                            before(kk)
                        i = three(bank[:, 4 + 2 * (j % 2) + b // 4, 0:T], j % RING, b, hh[:, kk, :], hl[:, kk, :],
                                  kk == 0, kk == 3)
                    i.then_inc(chunk_used.sem, 1)

            pe.sem_inc(chunk_used.sem, RING)
            pe.sem_inc(bank_empty.sem, 4)
            pe.sem_inc(pair_empty.sem, 2)
            pe.wait_ge(tab_loaded, 16)

            with pe.Fori(0, DEPTH) as l:
                c0 = l * CHUNKS
                t0 = l * TILES

                def sum_squares(n):
                    on("x_added", l, 4 * n)
                    pe.matmul(bank[:, 4, 0:T], ones, ssq[:, :], start=True, stop=True).then_inc(S["sum_sq"].sem, 1)

                def turn_kv():
                    on("k_rope", l)
                    pe.wait_ge(bank_empty.sem, bank_empty.at(l, 20))
                    for src, b0 in ((k, 4), (v, 6)):
                        for c in range(2):
                            for h in range(HEADS):
                                i = pe.transpose(bank[:, b0 + c, h * P:(h + 1) * P], src[:, h, c * CH:(c + 1) * CH], ident)
                    i.then_inc(S["kv_turned"].sem, 1)

                def scores():
                    on("kt_ready", l)
                    on("vt_ready", l)
                    for c in range(2):
                        for h in range(HEADS):
                            pe.matmul(bank[:, 4 + c, h * P:(h + 1) * P], k[:, h, c * CH:(c + 1) * CH],
                                      q[:, h, c * CH:(c + 1) * CH], start=True, stop=True)
                    for b0, src in ((6, k), (7, v)):
                        for h in range(HEADS):
                            i = pe.transpose(bank[0:B, b0, h * P:(h + 1) * P], src[:, h, SEQ:T], ident)
                    i.then_inc(S["scored"].sem, 1)

                def chunk_states():
                    on("kv8_ready", l)
                    for c in range(2):
                        for h in range(HEADS):
                            i = pe.matmul(bank[:, 6 + c, h * P:(h + 1) * P], kt_v[:, c, h, :], vt_v[:, c, h, :],
                                          start=True, stop=True)
                    i.then_inc(S["s_summed"].sem, 1)

                def outputs():
                    on("probs", l)
                    on("s1_ready", l)
                    for h in range(HEADS):
                        pe.matmul(bank[:, 4, h * P:(h + 1) * P], vt_v[:, 0, h, :], pt_v[:, 0, h, :], start=True, stop=True)
                    for h in range(HEADS):
                        pe.matmul(bank[:, 5, h * P:(h + 1) * P], vt_v[:, 1, h, :], pt_v[:, 1, h, :], start=True, stop=False)
                        i = pe.matmul(bank[:, 5, h * P:(h + 1) * P], s1_v[:, h, :], q[:, h, CH:2 * CH], start=False, stop=True)
                    i.then_inc(S["o_summed"].sem, 1)

                def outer(h):
                    on("v_diag", l, h + 1)
                    if h == 0:
                        on("o_ready", l)
                    else:
                        on("s_new", l, h)
                    for c in range(2):
                        i = pe.matmul(bank[:, 4 + c, :], kv8[:, 0, h, :],
                                      vd_v[:, 4 * c:4 * c + 4, :].rearrange("p b v -> p (b v)"), start=True, stop=True)
                    i.then_inc(S["outer"].sem, 1)

                def read_state(h):
                    on("s_new", l, h + 1)
                    for b in range(B):
                        i = pe.matmul(bank[:, 6, h * B + b:h * B + b + 1], states(h)[:, b, :],
                                      q[:, h, SEQ + b:SEQ + b + 1], start=True, stop=True)
                    if h == HEADS - 1:
                        i.then_inc(S["o8_summed"].sem, 1)
                    else:
                        i.then_inc(S["state_read"].sem, 1)

                def column_sums(src, ready, done):
                    def f():
                        on(ready, l)
                        for m in range(4):
                            i = pe.matmul(bank[:, 7, 0:T], ones, src[:, m, :], start=(m == 0), stop=(m == 3))
                        i.then_inc(S[done].sem, 1)
                    return f

                def head_sums():
                    on("o_sq", l)
                    on("ln_std", l)
                    for h in range(HEADS):
                        i = pe.matmul(bank[:, 4 + h, 0:T], ones, q[:, h, :], start=True, stop=True)
                    i.then_inc(S["o_sums"].sem, 1)

                def gates(g, free, done):
                    def f():
                        on("xr", l)
                        on(free, l)
                        pe.wait_ge(wg_loaded, l * 16 + 16)
                        for h in range(HEADS):
                            i = pe.matmul(bank[:, 4 + h, 0:T], wg[:, g, h, :], ag[:, h, :], start=True, stop=True)
                        i.then_inc(S[done].sem, 1)
                    return f

                hooks = {20: [turn_kv], 21: [scores], 22: [chunk_states], 24: [outputs],
                         25: [lambda: outer(0), column_sums(av, "conv_a", "ln_mean")],
                         26: [lambda: read_state(0), lambda: outer(1)], 27: [lambda: read_state(1)],
                         28: [column_sums(e, "ln_sq", "ln_var"), lambda: outer(2)],
                         29: [lambda: read_state(2), lambda: outer(3)],
                         31: [lambda: read_state(3)], 32: [head_sums],
                         34: [gates(0, "o_std", "ga")], 35: [gates(1, "r_sig", "gx")]}

                def norm_ready(base):
                    def f(kk):
                        pe.wait_ge(S["x_lo"].sem, base + (kk + 1))
                    return f

                group(c0, t0, xh, xl, {1: [lambda: sum_squares(0)]}, norm_ready(l * 32))
                with pe.Fori(1, 5) as g:
                    group(c0 + g * 8, t0 + g * 4, xh, xl)
                for g in range(5, 9):
                    group(c0 + g * 8, t0 + g * 4, xh, xl, {m: hooks.get(4 * g + m, ()) for m in range(4)})
                with pe.Fori(9, G_IN) as g:
                    group(c0 + g * 8, t0 + g * 4, xh, xl)

                def mixers_ready(kk):
                    if kk in (0, 4, 8):
                        on("mix_lo", l, {0: 1, 4: 3, 8: 2}[kk])
                    if kk >= 12:
                        on("mix_lo", l, kk - 8)
                group(c0 + G_IN * 8, t0 + G_IN * 4, mh, ml, None, mixers_ready)
                with pe.Fori(G_IN + 1, G_GATE0) as g:
                    group(c0 + g * 8, t0 + g * 4, mh, ml)
                group(c0 + G_GATE0 * 8, t0 + G_GATE0 * 4, xh, xl, {1: [lambda: sum_squares(1)]}, norm_ready(l * 32 + KT))
                on("std", l, 2)
                group(c0 + G_UP0 * 8, t0 + G_UP0 * 4, xh, xl)

                def hidden_ready(base):
                    def f(kk):
                        pe.wait_ge(S["h_lo"].sem, base + (kk + 1))
                    return f

                with pe.Fori(1, NBLK) as blk:
                    cb = c0 + blk * 24 + (G_LOOP - 3) * 8
                    tb = t0 + blk * 8 + (G_LOOP * 4 - 8)
                    group(cb, tb, xh, xl)
                    down(cb + 8, l * PAIRS + blk * 8 - 8, hidden_ready(l * (4 * NBLK) + blk * 4 - 4))
                    group(cb + 16, tb + 4, xh, xl)
                down(c0 + G_LAST * 8, l * PAIRS + (NBLK - 1) * 8, hidden_ready(l * (4 * NBLK) + (NBLK - 1) * 4))
            pe.wait_ge(S["x_added"].sem, S["x_added"].at(DEPTH - 1, 8))
            pe.matmul(bank[:, 4, 0:T], ones, ssq[:, :], start=True, stop=True).then_inc(final_sum, 1)

        GAMMA = [1.0 - 2.0 ** (-5.0 - h) for h in range(HEADS)]

        @block.vector
        def _(dve):
            tt, stt = dve.tensor_tensor, dve.scalar_tensor_tensor

            def on(name, l, kk=1):
                dve.wait_ge(S[name].sem, S[name].at(l, kk))

            def take(l, p, dst):
                dve.wait_ge(chunk_used.sem, chunk_used.at(l, 2 * p + 2))
                tt(dst, bank[:, p % 4, 0:T], rs[:, :], ALU.mult).then_inc(bank_empty.sem, 1)

            def taps(dst, src, weight, width, js):
                for n in js:
                    j = width - 1 - n
                    for m in range(4):
                        if n == 0:
                            dve.tensor_scalar(dst[:, m, 0:SEQ], src[:, m, 0:SEQ], weight(m, j), None, ALU.mult)
                        else:
                            stt(dst[:, m, n:SEQ], src[:, m, 0:SEQ - n], weight(m, j), dst[:, m, n:SEQ], ALU.mult, ALU.add)
                    i = dve.drain()
                return i

            def sample_conv(dst, window, weights, prod, width):
                tt(prod, window, weights.unsqueeze(2).broadcast_to([P, 4, B, width]), ALU.mult)
                dve.drain()
                dve.tensor_reduce(dst, prod, AX, ALU.add)

            def split_x(l, n, kk, gain):
                dve.wait_ge(S["x_hi"].sem, S["x_hi"].at(l, n + kk + 1))
                stt(xl[:, kk, :], x[:, kk, :], gain(kk), xh[:, kk, :].bitcast(F32), ALU.mult, ALU.subtract)\
                    .then_inc(S["x_lo"].sem, 1)

            def add_squares(n, squared_by_act=None):
                if squared_by_act is None:
                    dve.drain()
                    tt(e[:, :, :], x[:, 4 * n:4 * n + 4, :], x[:, 4 * n:4 * n + 4, :], ALU.mult)
                    dve.drain()
                else:
                    dve.wait_ge(S["x_sq"].sem, S["x_sq"].at(squared_by_act, n + 1))
                tt(e[:, 0:2, :], e[:, 0:2, :], e[:, 2:4, :], ALU.add)
                dve.drain()
                if n == 0:
                    tt(ssq[:, :], e[:, 0, :], e[:, 1, :], ALU.add).then_inc(S["x_added"].sem, 1)
                else:
                    tt(ssq[:, :], ssq[:, :], e[:, 0, :], ALU.add)
                    dve.drain()
                    tt(ssq[:, :], ssq[:, :], e[:, 1, :], ALU.add).then_inc(S["x_added"].sem, 1)

            dve.wait_ge(gains_loaded, 16)
            for kk in range(KT):
                dve.wait_ge(x_loaded[kk // 4], 16)
                split_x(-1, KT, kk, lambda t: gains[:, 0, t:t + 1])
            for n in range(4):
                add_squares(n)
            dve.wait_ge(tab_loaded, 16)

            with dve.Fori(0, DEPTH) as l:
                def gain(n):
                    return lambda t: gains[:, bass.ds(l * 2 + n, 1), t:t + 1].rearrange("p a b -> p (a b)")

                def rows(name):
                    return par[:, :, PAR[name][0]:PAR[name][1]]

                def rms(n):
                    on("std", l, n + 1)
                    dve.reciprocal(rs[:, :], std[:, :])
                    dve.drain()

                def mix_lo(n, t0, nt, src):
                    on("mix_hi", l, n + 1)
                    tt(ml[:, t0:t0 + nt, :], src, mh[:, t0:t0 + nt, :].bitcast(F32), ALU.subtract)\
                        .then_inc(S["mix_lo"].sem, 1)

                def wide(table):
                    return table.unsqueeze(1).broadcast_to([P, 4, T])

                def decay_rates():
                    on("lam_exp", l)
                    ts = dve.tensor_scalar
                    ts(sp[:, 3, :], sp[:, 1, :], 2.0, None, ALU.add)
                    dve.drain()
                    dve.reciprocal(sp[:, 4, :], sp[:, 3, :])
                    dve.drain()
                    tt(sp[:, 3, :], sp[:, 4, :], sp[:, 1, :], ALU.mult)
                    dve.drain()
                    tt(sp[:, 4, :], sp[:, 3, :], sp[:, 3, :], ALU.mult)
                    dve.drain()
                    ts(sp[:, 5, :], sp[:, 4, :], 1.0 / 17.0, None, ALU.mult)
                    dve.drain()
                    for n in range(7, 0, -1):
                        stt(sp[:, 5, :], sp[:, 5, :], 1.0 / (2 * n + 1), sp[:, 4, :], ALU.add, ALU.mult)
                        dve.drain()
                    stt(sp[:, 5, :], sp[:, 5, :], 1.0, sp[:, 3, :], ALU.add, ALU.mult)
                    ts(sp[:, 2, :], sp[:, 2, :], 0.0, None, ALU.max)
                    dve.drain()
                    stt(sp[:, 2, :], sp[:, 5, :], 2.0, sp[:, 2, :], ALU.mult, ALU.add)
                    dve.drain()
                    ts(sp[:, 6, :], sp[:, 2, :], 8.0, None, ALU.mult)
                    ts(sp[:, 7, :], sp[:, 2, :], -8.0, None, ALU.mult)

                def glu(m):
                    def f():
                        on("ag_sig", l, m + 1)
                        tt(u[:, m, :], av[:, m, :], ag[:, m, :], ALU.mult)
                    return f

                def conv_a_samples():
                    dve.drain()
                    dve.wait_ge(sa_loaded, l * 16 + 16)
                    dve.tensor_copy(sa_v[:, :, :, WA - 1], u[:, :, SEQ:T])
                    dve.tensor_copy(rows("pa"), u[:, :, SEQ - (WA - 1):SEQ])
                    dve.drain().then_inc(S["u_ready"].sem, 1)
                    sample_conv(av[:, :, SEQ:T], sa_v, rows("wa"), prod_a, WA)

                def conv_a(n):
                    def f():
                        i = taps(av, u, lambda m, j: pw("wa", m, j), WA, range(2 * n, min(2 * n + 2, WA)))
                        if n == 15:
                            i.then_inc(S["conv_a"].sem, 1)
                    return f

                def rope(t, swapped, done, scale):
                    def f():
                        on(swapped, l)
                        stt(e[:, :, :], ag[:, :, :], scale, wide(sin_t), ALU.mult, ALU.mult)
                        stt(t[:, :, :], t[:, :, :], scale, wide(cos_t), ALU.mult, ALU.mult)
                        dve.drain()
                        tt(t[:, :, :], t[:, :, :], e[:, :, :], ALU.add).then_inc(S[done].sem, 1)
                    return f

                def keys():
                    on("kv_turned", l)
                    tt(kt_v, bank[:, 4:6, :].rearrange("p c (h d) -> p c h d", h=HEADS),
                       decay_t.unsqueeze(1).unsqueeze(3).broadcast_to([P, 2, HEADS, CH]), ALU.mult)\
                        .then_inc(S["kt_ready"].sem, 1)

                def masked():
                    on("scored", l)
                    tt(pt_v, bank[:, 4:6, :].rearrange("p c (h i) -> p c h i", h=HEADS),
                       mask_t.unsqueeze(1).broadcast_to([P, 2, HEADS, CH]), ALU.mult)
                    tt(q[:, :, CH:2 * CH], q[:, :, CH:2 * CH], inner_t, ALU.mult)
                    dve.drain().then_inc(S["probs"].sem, 1)

                def prompt_states():
                    on("s_summed", l)
                    dve.tensor_copy(s1_v, bank[:, 6, :].rearrange("p (h d) -> p h d", h=HEADS))
                    dve.drain()
                    for h in range(HEADS):
                        stt(rp_v[:, h, :], s1_v[:, h, :], GAMMA[h] ** CH, bank[:, 7, h * P:(h + 1) * P], ALU.mult, ALU.add)
                    dve.drain().then_inc(S["s1_ready"].sem, 1)

                def v_diag(h):
                    if h:
                        on("outer", l, h)
                    else:
                        on("kv8_ready", l)
                    tt(vd_v, kv8[:, 1, h, :].unsqueeze(1).broadcast_to([B, B, CH]),
                       batch_t.unsqueeze(2).broadcast_to([B, B, CH]), ALU.mult).then_inc(S["v_diag"].sem, 1)

                def s_new(h):
                    def f():
                        on("outer", l, h + 1)
                        if h < HEADS - 1:
                            v_diag(h + 1)
                        dve.wait_ge(s_loaded[h % 2], l * 32 + (h // 2) * 16 + 16)
                        for c in range(2):
                            s = states(h)[:, 4 * c:4 * c + 4, :]
                            stt(s, s, GAMMA[h], bank[:, 4 + c, :].rearrange("p (b v) -> p b v", b=4), ALU.mult, ALU.add)
                        dve.drain().then_inc(S["s_new"].sem, 1)
                    return f

                def conv_c():
                    dve.wait_ge(rp_stored, l * 16 + 16)
                    sc = rows("sc").rearrange("p m (b j) -> p m b j", b=B)
                    dve.tensor_copy(sc[:, :, :, WC - 1], cx[:, :, SEQ:T])
                    dve.tensor_copy(rows("pc"), cx[:, :, SEQ - (WC - 1):SEQ])
                    dve.drain()
                    small = tmp[:, 0:HEADS * B * WC].rearrange("p (m b j) -> p m b j", m=HEADS, b=B)
                    sample_conv(ag[:, :, SEQ:T], sc, rows("wc"), small, WC)
                    taps(ag, cx, lambda m, j: pw("wc", m, j), WC, range(WC))
                    for m in range(4):
                        dve.tensor_scalar(ag[:, m, :], ag[:, m, :], pw("bc", m), None, ALU.add)
                    dve.drain().then_inc(S["xr"].sem, 1)

                def ln_center():
                    on("ln_mean", l)
                    for m in range(4):
                        stt(av[:, m, :], bank[:, 7, 0:T], -1.0 / W_GROUP, av[:, m, :], ALU.mult, ALU.add)
                    dve.drain().then_inc(S["centered"].sem, 1)

                def ln_scale():
                    on("ln_std", l)
                    dve.reciprocal(std[:, :], std[:, :])
                    dve.drain()
                    tt(av[:, :, :], av[:, :, :], wide(std[:, :]), ALU.mult).then_inc(S["ln_scaled"].sem, 1)

                def head_norm():
                    on("o_std", l)
                    on("dg_silu", l)
                    tt(v[:, :, :], v[:, :, :], dg[:, :, :], ALU.mult)
                    dve.reciprocal(e[:, :, :], e[:, :, :])
                    dve.drain()
                    tt(v[:, :, :], v[:, :, :], e[:, :, :], ALU.mult).then_inc(S["yd"].sem, 1)

                def gated_in():
                    on("i_sig", l)
                    tt(k[:, :, :], k[:, :, :], ag[:, :, :], ALU.mult).then_inc(S["ixr"].sem, 1)

                def b_square():
                    on("t_tanh", l)
                    dve.tensor_scalar(q[:, :, :], e[:, :, :], 1.0, None, ALU.add)
                    dve.drain()
                    dve.reciprocal(q[:, :, :], q[:, :, :])
                    dve.drain()
                    stt(q[:, :, :], e[:, :, :], 2.0, q[:, :, :], ALU.mult, ALU.mult)
                    dve.drain()
                    dve.tensor_scalar(q[:, :, :], q[:, :, :], 0.0, None, ALU.max).then_inc(S["b_sq"].sem, 1)

                def recur():
                    on("b_sqrt", l)
                    on("a_exp", l)
                    tt(k[:, :, :], k[:, :, :], q[:, :, :], ALU.mult)
                    tt(e[:, :, SEQ:T], ag[:, :, SEQ:T], rows("lru"), ALU.mult)
                    dve.drain()
                    tt(e[:, :, SEQ:T], e[:, :, SEQ:T], k[:, :, SEQ:T], ALU.add)
                    for m in range(4):
                        dve.tensor_tensor_scan(e[:, m, 0:SEQ], ag[:, m, 0:SEQ], k[:, m, 0:SEQ], 0.0, ALU.mult, ALU.add)
                    dve.drain()
                    dve.tensor_copy(rows("lru"), e[:, :, SEQ:T])
                    dve.tensor_copy(rows("pl"), e[:, :, SEQ - 1:SEQ])
                    dve.drain()
                    on("cg_gelu", l)
                    tt(e[:, :, :], e[:, :, :], cg[:, :, :], ALU.mult).then_inc(S["yc"].sem, 1)

                def conv_b():
                    dve.drain()
                    sbv = rows("sb").rearrange("p m (b j) -> p m b j", b=B)
                    dve.tensor_copy(sbv[:, :, :, WB - 1], cx[:, :, SEQ:T])
                    dve.tensor_copy(rows("pb"), cx[:, :, SEQ - (WB - 1):SEQ])
                    dve.drain()
                    small = tmp[:, 0:HEADS * B * WB].rearrange("p (m b j) -> p m b j", m=HEADS, b=B)
                    sample_conv(u[:, :, SEQ:T], sbv, rows("wb"), small, WB)
                    taps(u, cx, lambda m, j: pw("wb", m, j), WB, range(WB))

                after = {3: [decay_rates], 5: [glu(0)], 6: [glu(1)], 7: [glu(2)],
                         8: [glu(3), conv_a_samples], 12: [rope(q, "q_swap", "q_rope", 1.0)],
                         16: [rope(k, "k_swap", "k_rope", CH ** -0.5)], 20: [keys], 21: [masked],
                         22: [prompt_states], 24: [lambda: v_diag(0), conv_c], 26: [s_new(0), ln_center],
                         27: [s_new(1)], 28: [s_new(2)], 29: [s_new(3)], 30: [ln_scale],
                         31: [lambda: mix_lo(0, 0, 4, av[:, :, :])], 34: [head_norm], 36: [gated_in],
                         37: [b_square, lambda: mix_lo(1, 4, 4, v[:, :, :])], 39: [conv_b, recur]}
                for n in range(16):
                    after.setdefault(8 + n, []).append(conv_a(n))
                into = [av, ag, q, k, v, cx, cg, dg, cx]

                dve.wait_ge(par_loaded, l * 16 + 16)
                lam = rows("lam").rearrange("p m a -> p (m a)")
                dve.tensor_scalar(sp[:, 2, :], lam, -1.0, None, ALU.mult)
                dve.drain()
                tt(sp[:, 0, :], lam, sp[:, 2, :], ALU.min).then_inc(S["exp_in"].sem, 1)
                rms(0)
                for p in range(36):
                    take(l, p, into[p // 4][:, p % 4, :])
                    for f in after.get(p, ()):
                        f()
                for p in range(36, 40):
                    m = p % 4
                    take(l, p, one_tile[m % 2])
                    dve.drain()
                    tt(cx[:, m, :], cx[:, m, :], one_tile[m % 2], ALU.mult)
                    for f in after.get(p, ()):
                        f()
                for p in range(40, 44):
                    m = p % 4
                    take(l, p, one_tile[m % 2])
                    dve.drain()
                    tt(u[:, m, :], u[:, m, :], one_tile[m % 2], ALU.mult).then_inc(S["yb"].sem, 1)
                    if m == 0:
                        mix_lo(2, 8, 4, e[:, :, :])
                    else:
                        mix_lo(2 + m, 11 + m, 1, u[:, m - 1:m, :])
                mix_lo(6, 15, 1, u[:, 3:4, :])

                for kk in range(KT):
                    p = 44 + kk
                    dve.wait_ge(chunk_used.sem, chunk_used.at(l, 2 * p + 2))
                    tt(x[:, kk, :], x[:, kk, :], bank[:, p % 4, 0:T], ALU.add).then_inc(bank_empty.sem, 1)
                    if kk:
                        split_x(l, 0, kk - 1, gain(1))
                    if kk % 4 == 3:
                        if kk == KT - 1:
                            split_x(l, 0, kk, gain(1))
                        add_squares(kk // 4)

                def gate_tile(chunk, m):
                    dve.wait_ge(chunk_used.sem, chunk + (2 * m + 2 + RING))
                    tt(q[:, m, :], bank[:, m, 0:T], rs[:, :], ALU.mult).then_inc(bank_empty.sem, 1)

                def gate_conv(f0, between=lambda n: None):
                    f4 = bass.ds(f0, 4)
                    dve.drain()
                    dve.tensor_copy(fs_v[:, f4, :, WF - 1], q[:, :, SEQ:T])
                    dve.tensor_copy(fp[:, f4, :], q[:, :, SEQ - 2:SEQ])
                    dve.drain()
                    small = tmp[:, 0:4 * B * WF].rearrange("p (m b j) -> p m b j", m=4, b=B)
                    sample_conv(k[:, :, SEQ:T], fs_v[:, f4, :, :], wf[:, f4, :], small, WF)
                    for n in range(WF):
                        i = taps(k, q, lambda m, j: wf[:, bass.ds(f0 + m, 1), j:j + 1].rearrange("p a b -> p (a b)"), WF, [n])
                        if n == WF - 1:
                            i.then_inc(S["gate_conv"].sem, 1)
                        between(n)

                def up_tile(chunk, blk, m):
                    dve.wait_ge(chunk_used.sem, chunk + (2 * m + 2 + RING))
                    tt(one_tile[m % 2], bank[:, m, 0:T], rs[:, :], ALU.mult).then_inc(bank_empty.sem, 1)
                    dve.drain()
                    if m == 0:
                        dve.wait_ge(S["gate_silu"].sem, S["gate_silu"].at(l, blk + 1))
                    tt(v[:, m, :], k[:, m, :], one_tile[m % 2], ALU.mult).then_inc(S["h_new"].sem, 1)

                def h_low(blk, m):
                    dve.wait_ge(S["h_hi"].sem, S["h_hi"].at(l, blk * 4 + (m + 1)))
                    tt(hl[:, m, :], v[:, m, :], hh[:, m, :].bitcast(F32), ALU.subtract).then_inc(S["h_lo"].sem, 1)

                def up_block(chunk, blk):
                    for m in range(4):
                        up_tile(chunk, blk, m)
                        if m:
                            h_low(blk, m - 1)
                    h_low(blk, 3)

                def down_pair(chunk, j):
                    dve.wait_ge(chunk_used.sem, chunk + (j + 1 + RING))
                    for n in range(2):
                        i = tt(x[:, 2 * j + n, :], x[:, 2 * j + n, :], bank[:, 4 + 2 * (j % 2) + n, 0:T], ALU.add)
                    dve.drain().then_inc(pair_empty.sem, 1)

                rms(1)
                dve.wait_ge(fs_loaded, l * 16 + 16)
                dve.wait_ge(wf_loaded, l * 16 + 16)
                c0 = l * CHUNKS
                for m in range(4):
                    gate_tile(c0 + G_GATE0 * 8, m)
                gate_conv(0)
                up_block(c0 + G_UP0 * 8, 0)
                with dve.Fori(1, NBLK) as blk:
                    cb = c0 + blk * 24 + (G_LOOP - 3) * 8
                    for m in range(4):
                        gate_tile(cb, m)
                    gate_conv(blk * 4, lambda n: down_pair(cb + 8, n - 1) if n else None)
                    for j in range(2, 8):
                        down_pair(cb + 8, j)
                    up_block(cb + 16, blk)
                for j in range(8):
                    down_pair(c0 + G_LAST * 8, j)
                    if j:
                        split_x(l, KT, 2 * j - 2, gain(2))
                        split_x(l, KT, 2 * j - 1, gain(2))
                    if j in (3, 5, 7):
                        add_squares((3, 5, 7).index(j), l)
                split_x(l, KT, KT - 2, gain(2))
                split_x(l, KT, KT - 1, gain(2))
                add_squares(3, l)

            dve.wait_ge(final_std, 1)
            dve.reciprocal(rs[:, :], std[:, :])
            dve.drain()
            for n in range(4):
                for kk in range(4 * n, 4 * n + 4):
                    stt(x[:, kk, :], x[:, kk, :], gains[:, 2 * DEPTH, kk:kk + 1], rs[:, :], ALU.mult, ALU.mult)
                dve.drain().then_inc(y_ready, 1)


def _tables(np):
    half = P // 2
    inv = np.float32(10000.0) ** (-np.arange(half, dtype=np.float32) / np.float32(half))
    pos = np.concatenate([np.arange(SEQ), np.full(B, 2048)]).astype(np.float32)
    ang = (inv[:, None] * pos[None, :]).astype(np.float32).astype(np.float64)
    cos = np.concatenate([np.cos(ang), np.cos(ang)])
    sin = np.concatenate([-np.sin(ang), np.sin(ang)])
    log_g = np.log(1.0 - 2.0 ** (-5.0 - np.arange(HEADS)))
    i = np.arange(CH)
    rel = i[None, :] - i[:, None]
    mask = np.where(rel[:, None, :] >= 0, np.exp(log_g[None, :, None] * np.maximum(rel, 0)[:, None, :]), 0.0)
    inner = np.broadcast_to(np.exp(log_g[:, None] * (i + 1.0)[None, :])[None], (P, HEADS, CH))
    decay = np.exp(log_g[None, :] * (CH - 1.0 - i)[:, None])
    batch = np.zeros((P, B)); batch[:B, :] = np.eye(B)
    parts = [cos, sin, mask.reshape(P, -1), inner.reshape(P, -1), decay, batch, np.eye(P), np.ones((P, P)), np.full((P, 1), EPS)]
    return np.ascontiguousarray(np.concatenate(parts, axis=1).astype(np.float32))


def _channels(np, a):
    a = np.moveaxis(a, -1, 0)
    return np.moveaxis(a.reshape(a.shape[0] // P, P, *a.shape[1:]), 0, 1)


def _chunks(np, w, first, count, rows=None):
    k = w.shape[0] // P
    t = w[:, first:first + count * P].reshape(k, P, count, P)
    if rows is not None:
        t = t[rows]
    t = t.transpose(2, 0, 1, 3)
    return t.reshape(-1, 8, P, P).transpose(0, 2, 1, 3).reshape(-1, P, CHUNK)


def kernel(**inputs):
    import numpy as np
    import concourse.bacc as bacc
    from concourse.bass_utils import run_bass_kernel_spmd

    a = {n: np.asarray(v) for n, v in inputs.items()}
    x = np.concatenate([a["x_prompt"][0], a["x_sample"][:, 0]], axis=0)
    weights = np.empty((DEPTH * CHUNKS, P, CHUNK), np.float32)
    at = 0
    for l in range(DEPTH):
        def put(w, first, count, rows=None):
            nonlocal at
            c = _chunks(np, w, first, count, rows)
            weights[at:at + len(c)] = c
            at += len(c)
        for g in IN_ORDER:
            put(a["w_in"][l], g * W_GROUP, 4)
        put(a["w_out"][l], 0, KT, OUT_ROWS)
        for blk in range(NBLK):
            put(a["w_ffn_gate"][l], blk * 512, 4)
            if blk:
                put(a["w_ffn_down"][l][(blk - 1) * 512:blk * 512], 0, KT)
            put(a["w_ffn_up"][l], blk * 512, 4)
        put(a["w_ffn_down"][l][(NBLK - 1) * 512:], 0, KT)

    par = np.zeros((DEPTH, P, HEADS, N_PAR_IN), np.float32)
    sa = np.zeros((DEPTH, P, HEADS, B, WA), np.float32)
    wf = np.zeros((DEPTH, P, FT, WF), np.float32)
    fs = np.zeros((DEPTH, P, FT, B, WF), np.float32)
    wg = np.zeros((DEPTH, P, 2, HEADS, P), np.float32)
    sr = np.ascontiguousarray(a["state_ret_d"].transpose(0, 2, 3, 1, 4)).reshape(DEPTH * HEADS, P, B, CH)
    for l in range(DEPTH):
        for name, src in (("wa", "w_conv_a"), ("wb", "w_conv_b"), ("wc", "w_conv_c")):
            par[l, :, :, slice(*PAR[name])] = _channels(np, a[src][l])
        for name, src in (("bc", "b_conv_c"), ("lng", "ln_a_g"), ("lnb", "ln_a_b"), ("ba", "b_gate_a"),
                          ("bx", "b_gate_x"), ("lam", "lru_lambda")):
            par[l, :, :, PAR[name][0]] = _channels(np, a[src][l])
        for name, src, w in (("sb", "state_conv_b", WB), ("sc", "state_conv_c", WC)):
            s = np.zeros((P, HEADS, B, w), np.float32)
            s[..., :w - 1] = _channels(np, a[src][l])
            par[l, :, :, slice(*PAR[name])] = s.reshape(P, HEADS, B * w)
        par[l, :, :, slice(*PAR["lru"])] = _channels(np, a["state_lru_c"][l])
        sa[l, ..., :WA - 1] = _channels(np, a["state_conv_a"][l])
        wf[l] = _channels(np, a["w_conv_ffn"][l])
        fs[l, ..., :WF - 1] = _channels(np, a["state_conv_ffn"][l])
        for n, src in enumerate(("w_gate_a", "w_gate_x")):
            wg[l, :, n] = a[src][l].transpose(1, 0, 2)
    gains = np.stack([a["g_mix"][0], a["g_ffn"][0], a["g_mix"][1], a["g_ffn"][1], a["g_final"]])
    arrays = {
        "x_in": np.ascontiguousarray(_channels(np, x)), "weights": weights, "params": par,
        "conv_a_state": sa.reshape(DEPTH, P, -1), "gate_weights": wg.reshape(DEPTH, P, -1), "ret_state": sr,
        "ffn_taps": wf, "ffn_state": fs.reshape(DEPTH, P, -1),
        "gains": np.ascontiguousarray(gains.reshape(2 * DEPTH + 1, KT, P).transpose(2, 0, 1)), "tables": _tables(np),
    }
    outs = {
        "y": (P, KT, T), "new_params": (DEPTH, P, HEADS, N_PAR - STATE0), "new_conv_a": (DEPTH, P, HEADS * B * WA),
        "new_ret_prompt": (DEPTH, P, HEADS, CH), "new_ret_sample": (DEPTH * HEADS, P, B, CH),
        "new_ffn_sample": (DEPTH, P, FT * B * WF), "new_ffn_prompt": (DEPTH, P, FT, 2),
    }
    nc = bacc.Bacc("TRN2", target_bir_lowering=False, num_devices=1)
    args = [nc.dram_tensor("in_" + n, v.shape, F32, kind="ExternalInput").ap() for n, v in arrays.items()]
    args += [nc.dram_tensor("out_" + n, s, F32, kind="ExternalOutput").ap() for n, s in outs.items()]
    hybrid_step(nc, *args)
    got = run_bass_kernel_spmd(nc, [{"in_" + n: v for n, v in arrays.items()}], core_ids=[0]).results[0]
    r = {n: got["out_" + n] for n in outs}

    def rows(t, lead):
        t = np.moveaxis(t, (lead, lead + 1), (-1, -2))
        return t.reshape(*t.shape[:-2], -1)

    y = rows(r["y"], 0)
    new = r["new_params"]

    def part(name, *shape):
        lo, hi_ = (n - STATE0 for n in PAR[name])
        return rows(new[..., lo:hi_].reshape(DEPTH, P, HEADS, *shape), 1)

    sa_n = rows(r["new_conv_a"].reshape(DEPTH, P, HEADS, B, WA), 1)[:, :, 1:]
    fs_n = rows(r["new_ffn_sample"].reshape(DEPTH, P, FT, B, WF), 1)[:, :, 1:]
    out = (
        y[None, :SEQ], y[SEQ:, None], part("pa", WA - 1)[:, None], part("pb", WB - 1)[:, None],
        part("pc", WC - 1)[:, None], part("pl", 1), r["new_ret_prompt"].transpose(0, 2, 1, 3)[:, None],
        rows(r["new_ffn_prompt"], 1)[:, None], sa_n, part("sb", B, WB)[:, :, 1:], part("sc", B, WC)[:, :, 1:],
        part("lru", B), r["new_ret_sample"].reshape(DEPTH, HEADS, P, B, CH).transpose(0, 3, 1, 2, 4), fs_n,
    )
    return tuple(np.ascontiguousarray(o) for o in out)
```
